# Optimizing a Trainium2 kernel written in Bass

```python
import jax, jax.numpy as jnp
from jax import lax
import numpy as np

D_MODEL = 2048
BATCH = 1
SEQ = 256
DEPTH = 1

CHUNK = 64
D_HGRN = D_MODEL // 2
HGRN_HEAD_DIM = 128
HGRN_HEADS = D_HGRN // HGRN_HEAD_DIM
D_POOL = D_MODEL - D_HGRN
POOL_WINDOWS = (2, 4, 8, 16)
N_POOL_GROUPS = len(POOL_WINDOWS)
POOL_GROUP_DIM = D_POOL // N_POOL_GROUPS
D_IN = 4 * D_HGRN + D_POOL
D_FF = 5632
RMS_EPS = 1e-6

kernel_name = "hymba_style_hgrn2_pool_macaron_block"

def rmsnorm(x, gain):
    x32 = x.astype(jnp.float32)
    y = x32 * lax.rsqrt(jnp.mean(x32 * x32, axis=-1, keepdims=True) + RMS_EPS)
    return (y * gain.astype(jnp.float32)).astype(x.dtype)

def swiglu(h, w_gate, w_up, w_down):
    return (jax.nn.silu(h @ w_gate) * (h @ w_up)) @ w_down

def hgrn2_mixer(q, f_logit, i, g, lb, g_norm):
    b_sz, t_len, _ = q.shape
    n_chunks = t_len // CHUNK
    f = lb.astype(jnp.float32) + (1.0 - lb.astype(jnp.float32)) * jax.nn.sigmoid(f_logit.astype(jnp.float32))
    log_f = jnp.log(f)
    k = 1.0 - f

    def to_chunks(a):
        a = a.astype(jnp.float32).reshape(b_sz, n_chunks, CHUNK, HGRN_HEADS, HGRN_HEAD_DIM)
        return a.transpose(1, 0, 3, 2, 4)

    qs, ks, vs, gs = to_chunks(q), to_chunks(k), to_chunks(i), to_chunks(log_f)
    causal = jnp.tril(jnp.ones((CHUNK, CHUNK), dtype=bool))

    def step(state, xs):
        qc, kc, vc, gc = xs
        cum = jnp.cumsum(gc, axis=2)
        diff = cum[:, :, :, None, :] - cum[:, :, None, :, :]
        decay = jnp.exp(jnp.where(causal[None, None, :, :, None], diff, -jnp.inf))
        scores = jnp.einsum('bhtd,bhsd,bhtsd->bhts', qc, kc, decay)
        o_intra = jnp.einsum('bhts,bhsv->bhtv', scores, vc)
        o_inter = jnp.einsum('bhtk,bhkv->bhtv', qc * jnp.exp(cum), state)
        last = cum[:, :, -1:, :]
        new_state = jnp.exp(last[:, :, 0, :])[..., None] * state + jnp.einsum(
            'bhsk,bhsv->bhkv', kc * jnp.exp(last - cum), vc)
        return new_state, o_intra + o_inter

    state0 = jnp.zeros((b_sz, HGRN_HEADS, HGRN_HEAD_DIM, HGRN_HEAD_DIM), jnp.float32)
    _, o = lax.scan(step, state0, (qs, ks, vs, gs))
    o = o.transpose(1, 0, 3, 2, 4).reshape(b_sz, t_len, HGRN_HEADS, HGRN_HEAD_DIM)
    o = rmsnorm(o, g_norm).reshape(b_sz, t_len, D_HGRN)
    return (o * jax.nn.silu(g.astype(jnp.float32))).astype(q.dtype)

def pool_mixer(u, w_pool, pool_scale):
    t_len = u.shape[1]
    u32 = u.astype(jnp.float32)
    pos = jnp.arange(t_len, dtype=jnp.int32)
    outs = []
    for gi, w in enumerate(POOL_WINDOWS):
        seg = u32[..., gi * POOL_GROUP_DIM:(gi + 1) * POOL_GROUP_DIM]
        csum = jnp.cumsum(seg, axis=1)
        csum_prev = jnp.pad(csum, ((0, 0), (w, 0), (0, 0)))[:, :t_len]
        count = jnp.minimum(pos + 1, w).astype(jnp.float32)[None, :, None]
        pooled = (csum - csum_prev) / count - seg
        outs.append(jnp.einsum('btc,cd->btd', pooled, w_pool[gi].astype(jnp.float32)))
    y = jnp.concatenate(outs, axis=-1) * pool_scale.astype(jnp.float32)
    return y.astype(u.dtype)

def setup_inputs(seed: int = 0) -> dict:
    key = jax.random.key(seed)
    ks = jax.random.split(key, 20)
    n = jax.random.normal

    def gain(k, d):
        return 1.0 + 0.02 * n(k, (DEPTH, d), jnp.float32)

    return {
        "x": n(ks[0], (BATCH, SEQ, D_MODEL), jnp.float32),
        "ffn1_pre_g": gain(ks[1], D_MODEL),
        "ffn1_w_gate": n(ks[2], (DEPTH, D_MODEL, D_FF), jnp.float32) * D_MODEL ** -0.5,
        "ffn1_w_up": n(ks[3], (DEPTH, D_MODEL, D_FF), jnp.float32) * D_MODEL ** -0.5,
        "ffn1_w_down": n(ks[4], (DEPTH, D_FF, D_MODEL), jnp.float32) * D_FF ** -0.5,
        "ffn1_post_g": gain(ks[5], D_MODEL),
        "mix_pre_g": gain(ks[6], D_MODEL),
        "w_in": n(ks[7], (DEPTH, D_MODEL, D_IN), jnp.float32) * D_MODEL ** -0.5,
        "hgrn_lb_logits": n(ks[8], (DEPTH + 1, D_HGRN), jnp.float32),
        "hgrn_g_norm": gain(ks[9], HGRN_HEAD_DIM),
        "w_pool": n(ks[10], (DEPTH, N_POOL_GROUPS, POOL_GROUP_DIM, POOL_GROUP_DIM), jnp.float32) * POOL_GROUP_DIM ** -0.5,
        "pool_scale": gain(ks[11], D_POOL),
        "w_out": n(ks[12], (DEPTH, D_MODEL, D_MODEL), jnp.float32) * D_MODEL ** -0.5,
        "mix_post_g": gain(ks[13], D_MODEL),
        "ffn2_pre_g": gain(ks[14], D_MODEL),
        "ffn2_w_gate": n(ks[15], (DEPTH, D_MODEL, D_FF), jnp.float32) * D_MODEL ** -0.5,
        "ffn2_w_up": n(ks[16], (DEPTH, D_MODEL, D_FF), jnp.float32) * D_MODEL ** -0.5,
        "ffn2_w_down": n(ks[17], (DEPTH, D_FF, D_MODEL), jnp.float32) * D_FF ** -0.5,
        "ffn2_post_g": gain(ks[18], D_MODEL),
    }

def reference(x, ffn1_pre_g, ffn1_w_gate, ffn1_w_up, ffn1_w_down, ffn1_post_g,
              mix_pre_g, w_in, hgrn_lb_logits, hgrn_g_norm, w_pool, pool_scale,
              w_out, mix_post_g, ffn2_pre_g, ffn2_w_gate, ffn2_w_up, ffn2_w_down,
              ffn2_post_g):
    lb_all = jnp.cumsum(jax.nn.softmax(hgrn_lb_logits.astype(jnp.float32), axis=0), axis=0)
    split_at = [D_HGRN, 2 * D_HGRN, 3 * D_HGRN, 4 * D_HGRN]
    for l in range(DEPTH):
        h = swiglu(rmsnorm(x, ffn1_pre_g[l]), ffn1_w_gate[l], ffn1_w_up[l], ffn1_w_down[l])
        x = x + 0.5 * rmsnorm(h, ffn1_post_g[l])
        h = rmsnorm(x, mix_pre_g[l])
        proj = h @ w_in[l]
        q, f_logit, i, g, u = jnp.split(proj, split_at, axis=-1)
        y_rec = hgrn2_mixer(q, f_logit, i, g, lb_all[l], hgrn_g_norm[l])
        y_pool = pool_mixer(u, w_pool[l], pool_scale[l])
        y = jnp.concatenate([y_rec, y_pool], axis=-1) @ w_out[l]
        x = x + rmsnorm(y, mix_post_g[l])
        h = swiglu(rmsnorm(x, ffn2_pre_g[l]), ffn2_w_gate[l], ffn2_w_up[l], ffn2_w_down[l])
        x = x + 0.5 * rmsnorm(h, ffn2_post_g[l])
    return x


_drawn_inputs = setup_inputs


def setup_inputs(seed=0):
    import zlib

    import numpy as np

    out = dict(_drawn_inputs(seed))
    spreads = {}
    factors = {'ffn1_pre_g': 3.28,
     'ffn1_post_g': 4.731,
     'hgrn_g_norm': 24.148,
     'pool_scale': 18.369,
     'mix_post_g': 10.977,
     'ffn2_pre_g': 18.521,
     'ffn2_post_g': 35.168}
    for name, (base, spread) in spreads.items():
        noise = np.random.default_rng([zlib.crc32(name.encode()), seed]).standard_normal(out[name].shape)
        drawn = base * np.exp(spread * noise) if base else spread * noise
        out[name] = __import__('jax').numpy.asarray(drawn.astype(out[name].dtype))
    for name, factor in factors.items():
        out[name] = (out[name] * factor).astype(out[name].dtype)
    return out
```

```python
import concourse.bass as bass
from concourse import mybir
from concourse.alu_op_type import AluOpType as ALU
from contextlib import ExitStack

P = 128
SEQ, D, FF = 256, 2048, 5632
TOK = SEQ // P
KC = D // P
FC = FF // P
NT = 512
FTILES = FF // NT
DN = D // NT
DH = D // 2
HEADS = DH // P
INTILES = 5 * DH // NT
WINDOWS = (2, 4, 8, 16)
WMAX = max(WINDOWS)
EPS = 1e-6
LEVELS = (1, 2, 4, 8, 16, 32, 64)

RAW = 4
RING = 4
AHEAD = RING - 1

U1 = 0
D1 = U1 + 16 * FTILES
IN = D1 + 2 * FC
OUT = IN + 8 * INTILES
U2 = OUT + 2 * KC
D2 = U2 + 16 * FTILES
END = D2 + 2 * FC

G_FFN1, G_MIX, G_FFN2, LB0, LB1, PSC = 0, 16, 32, 48, 56, 64
VROWS = 72

TB = (4, 5, 6)
JUNK = 7


def build(nc, x_d, g1pre_d, w1g_d, w1u_d, w1d_d, g1post_d, mixpre_d, win_d, lb_d, gnorm_d,
          wpool_d, psc_d, wout_d, mixpost_d, g2pre_d, w2g_d, w2u_d, w2d_d, g2post_d, out_d):
    f32 = mybir.dt.float32
    f32r = mybir.dt.float32r
    i32 = mybir.dt.int32
    ACT = mybir.ActivationFunctionType
    AX = mybir.AxisListType
    K = 1024
    base = (nc.sbuf_base + 63) // 64 * 64

    def at(name, kib, shape, dt=f32):
        return nc.alloc_sbuf_tensor_at(name, shape, dt, offset=base + int(kib * K))

    raw = at("raw", 0, [P, RAW, 2048])
    whi = at("whi", 32, [P, RING, 1024], f32r)
    wlo = at("wlo", 48, [P, RING, 1024], f32r)
    hT_hi = at("hT_hi", 64, [P, FC, SEQ], f32r)
    hT_lo = at("hT_lo", 108, [P, FC, SEQ], f32r)
    xT_hi = at("xT_hi", 152, [P, KC, SEQ], f32r)
    xT_lo = at("xT_lo", 168, [P, KC, SEQ], f32r)
    x = at("x", 184, [P, TOK, D])
    nat = at("nat", 200, [P, TOK, NT])
    ident = at("ident", 204, [P, P])
    vrow = at("vrow", 204.5, [P, P])
    vcol = at("vcol", 205, [P, VROWS])
    ss = at("ss", 205.5, [P, 6, TOK, DN])
    ms = at("ms", 205.75, [P, 6, TOK])
    rr = at("rr", 205.875, [P, 6, TOK])
    mhalf = at("mhalf", 206, [P, TOK * HEADS])
    lbt = at("lbt", 206.125, [P, 6, HEADS])
    hss = at("hss", 206.375, [P, TOK, HEADS])
    hms = at("hms", 206.5, [P, TOK, HEADS])
    hrr = at("hrr", 206.625, [P, TOK, HEADS])
    yg = at("yg", 152, [P, DN, TOK, NT])
    gpost = at("gpost", 168, [P, D])
    yT_hi = hT_hi
    yT_lo = hT_lo
    T = at("T", 64, [P, HEADS, SEQ])
    pooledT = at("pooledT", 64, [P, HEADS, SEQ])
    u_sb = at("u_sb", 72, [P, TOK, DH])
    qP = at("qP", 80, [P, HEADS, SEQ])
    osq = at("osq", 80, [P, TOK, DH])
    kR = at("kR", 88, [P, HEADS, SEQ])
    orn = at("orn", 88, [P, TOK, DH])
    v_sb = at("v_sb", 96, [P, TOK, DH])
    mask = at("mask", 104, [P, len(LEVELS), P])
    wp_sb = at("wp_sb", 108, [P, 8, 256])
    S = at("S", 124, [P, HEADS, 3 * P])
    sg = at("sg", 136, [P, TOK, DH])
    band = at("band", 144, [P, len(WINDOWS), SEQ + P])
    gn_sb = at("gn_sb", 150.5, [P, P])

    with ExitStack() as ctx:
        ps = [ctx.enter_context(nc.psum_tensor(f"ps{i}", [P, NT], f32)) for i in range(8)]

        def sem(name):
            return ctx.enter_context(nc.semaphore(name))

        raw_in = [sem(f"raw_in{i}") for i in range(RAW)]
        hi_ready, lo_ready = sem("hi_ready"), sem("lo_ready")
        w_used = sem("w_used")
        x_in = [sem(f"x_in{i}") for i in range(2)]
        vec_in, gain_in, mixw_in = sem("vec_in"), sem("gain_in"), sem("mixw_in")
        ident_ok, consts_ok = sem("ident_ok"), sem("consts_ok")
        vcol_tr, vcol_ok = sem("vcol_tr"), sem("vcol_ok")
        silu_ok, h_ok = sem("silu_ok"), sem("h_ok")
        h_tr, h_hi, h_lo = sem("h_tr"), sem("h_hi"), sem("h_lo")
        y_free, y_sq = sem("y_free"), sem("y_sq")
        ms_ok, r_ok = sem("ms_ok"), sem("r_ok")
        xn_ok, x_sq = sem("xn_ok"), sem("x_sq")
        x_tr, x_hi, x_lo = sem("x_tr"), sem("x_hi"), sem("x_lo")
        dv, gp = sem("dv"), sem("gp")
        nat_ok, in_tr, in_ev, fk_ok = sem("nat_ok"), sem("in_tr"), sem("in_ev"), sem("fk_ok")
        lb_in, lb_exp = sem("lb_in"), sem("lb_exp")
        lev_ready, lev_done, s_last = sem("lev_ready"), sem("lev_done"), sem("s_last")
        o_done, o_sq, hms_ok, hr_ok, orn_ok = (sem(n) for n in ("o_done", "o_sq", "hms_ok", "hr_ok", "orn_ok"))
        pool_mm, pool_ev, wp_mm, yp_hi, yp_lo = (sem(n) for n in ("pool_mm", "pool_ev", "wp_mm", "yp_hi", "yp_lo"))
        yrec_ok, yr_tr, yr_hi, yr_lo = (sem(n) for n in ("yrec_ok", "yr_tr", "yr_hi", "yr_lo"))
        out_ok = sem("out_ok")

        block = ctx.enter_context(nc.Block())

        in_cols = [DH + NT * t for t in range(2)] + [NT * t for t in range(2)] + \
                  [2 * DH + NT * t for t in range(2)] + [4 * DH + NT * t for t in range(2)] + \
                  [3 * DH + NT * t for t in range(2)]
        out_kc = list(range(KC // 2, KC)) + list(range(KC // 2))

        def flat(ap):
            return ap.rearrange("p a b -> p (a b)")

        @block.sync
        def _(sp):
            def load(first_half, src, chunks, j=0):
                n = first_half // 2
                if not (isinstance(j, int) and first_half + 16 * j < 2 * RAW):
                    sp.wait_ge(lo_ready, j * 16 + (first_half - 2 * RAW + 2))
                dst = raw[:, n % RAW, :].rearrange("p (c f) -> p c f", c=chunks)
                sp.dma_start(dst, src).then_inc(raw_in[n % RAW], 16)

            def up_tile(b, j, wg, wu):
                for m, w in enumerate((wg, wu)):
                    rows = w[0].rearrange("(c p) f -> p c f", p=P)
                    for q in range(4):
                        load(b + 8 * m + 2 * q, rows[:, 4 * q:4 * q + 4, bass.ds(j * NT, NT)], 4, j)

            def up(b, wg, wu):
                up_tile(b, 0, wg, wu)
                with sp.Fori(1, FTILES) as j:
                    up_tile(b, j, wg, wu)

            def down(b, w, order):
                rows = w[0].rearrange("(c p) n -> p c n", p=P)
                for i in range(2):
                    for n in range(0, len(order), 2):
                        load(b + len(order) * i + n, rows[:, order[n]:order[n] + 2, 1024 * i:1024 * (i + 1)], 2)

            xv = x_d[0].rearrange("(t p) d -> p t d", p=P)
            for n in range(2):
                sp.dma_start(x[:, :, n * DH:(n + 1) * DH], xv[:, :, n * DH:(n + 1) * DH]).then_inc(x_in[n], 16)
            up(U1, w1g_d, w1u_d)
            down(D1, w1d_d, list(range(FC)))
            rows = win_d[0].rearrange("(c p) f -> p c f", p=P)
            for t in range(INTILES):
                for q in range(4):
                    load(IN + 8 * t + 2 * q, rows[:, 4 * q:4 * q + 4, in_cols[t]:in_cols[t] + NT], 4)
            down(OUT, wout_d, out_kc)
            up(U2, w2g_d, w2u_d)
            down(D2, w2d_d, list(range(FC)))
            ov = out_d[0].rearrange("(t p) d -> p t d", p=P)
            for n in range(DN):
                sp.wait_ge(xn_ok, TOK * DN * 2 + TOK * (n + 1))
                sp.dma_start(ov[:, :, n * NT:(n + 1) * NT], x[:, :, n * NT:(n + 1) * NT]).then_inc(out_ok, 16)
            sp.wait_ge(out_ok, 16 * DN)

        @block.gpsimd
        def _(pool):
            count = [0]

            def link(ins):
                count[0] += 1
                ins.then_inc(gp, 1)
                pool.wait_ge(gp, count[0])

            link(nc.gpsimd.memset(ident[:], 0.0))
            nc.gpsimd.affine_select(out=ident[:], in_=ident[:], compare_op=ALU.not_equal, fill=1.0, base=0,
                                    pattern=[[-1, P]], channel_multiplier=1).then_inc(ident_ok, 1)
            link(nc.gpsimd.memset(mhalf[:], -0.5))

            def inv_root(k, half):
                pool.wait_ge(ms_ok, k + 1)
                ins = nc.gpsimd.tensor_tensor(rr[:, k, :], ms[:, k, :], mhalf[:, 0:TOK], ALU.pow)
                if half:
                    link(ins)
                    ins = nc.gpsimd.tensor_scalar(rr[:, k, :], rr[:, k, :], 0.5, None, ALU.mult)
                ins.then_inc(r_ok, 1)

            def load_gain(b, gain):
                pool.wait_ge(w_used, b)
                pool.dma_start(gpost[:], gain[0:1, :].broadcast_to([P, D])).then_inc(gain_in, 16)

            inv_root(0, False)
            load_gain(D1, g1post_d)
            inv_root(1, True)
            pool.wait_ge(w_used, IN)
            pool.dma_start(gn_sb[:], gnorm_d[0:1, :].broadcast_to([P, P])).then_inc(mixw_in, 16)
            pool.dma_start(wp_sb[:], wpool_d[0].rearrange("g (c p) d -> p (g c) d", p=P)).then_inc(mixw_in, 16)
            inv_root(2, False)
            for wi, w in enumerate(WINDOWS):
                link(nc.gpsimd.memset(band[:, wi, :], 1.0 / w))
                for t in range(w - 1):
                    link(nc.gpsimd.memset(band[:, wi, t:t + 1], 1.0 / (t + 1)))
                for c0, n in ((0, SEQ), (SEQ, P)):
                    b = band[:, wi, c0:c0 + n]
                    link(nc.gpsimd.affine_select(out=b, in_=b, compare_op=ALU.is_ge, fill=0.0, base=0,
                                                 pattern=[[1, n]], channel_multiplier=-1))
                    link(nc.gpsimd.affine_select(out=b, in_=b, compare_op=ALU.is_ge, fill=0.0, base=w - 1,
                                                 pattern=[[-1, n]], channel_multiplier=1))
                    link(nc.gpsimd.tensor_tensor(b[:, 0:P], b[:, 0:P], ident[:], ALU.subtract))
            for li, m in enumerate(LEVELS):
                link(nc.gpsimd.memset(mask[:, li, :], 1.0))
                n = P // (2 * m)
                for blk in range(2):
                    v = mask[:, li, 64 * blk:64 * blk + 64].rearrange("p (j m) -> p j m", m=m)
                    link(nc.gpsimd.affine_select(out=v, in_=v, compare_op=ALU.is_ge, fill=0.0, base=0,
                                                 pattern=[[-2 * m, n], [0, m]], channel_multiplier=1))
                    ins = nc.gpsimd.affine_select(out=v, in_=v, compare_op=ALU.is_ge, fill=0.0, base=m - 1,
                                                  pattern=[[2 * m, n], [0, m]], channel_multiplier=-1)
                    if li < len(LEVELS) - 1 or blk == 0:
                        link(ins)
            ins.then_inc(consts_ok, 1)
            pool.wait_ge(hms_ok, 1)
            nc.gpsimd.tensor_tensor(flat(hrr[:]), flat(hms[:]), mhalf[:], ALU.pow).then_inc(hr_ok, 1)
            load_gain(OUT, mixpost_d)
            inv_root(3, False)
            inv_root(4, False)
            load_gain(D2, g2post_d)
            inv_root(5, True)

        @block.scalar
        def _(act):
            def hi(g, j=0):
                if isinstance(j, int) and g + 16 * j >= END:
                    return
                act.wait_ge(raw_in[g // 2 % RAW], j * 32 + 16 * (g // 2 // RAW + 1))
                if not (isinstance(j, int) and g + 16 * j < RING):
                    act.wait_ge(w_used, j * 16 + (g - RING + 1))
                nc.scalar.activation(whi[:, g % RING, :], raw[:, g // 2 % RAW, 1024 * (g % 2):1024 * (g % 2 + 1)],
                                     ACT.Copy).then_inc(hi_ready, 1)

            squares = {x_sq: 0, y_sq: 0}
            before = []

            def square(dst, src, signal):
                if before:
                    act.wait_ge(*before[-1])
                squares[signal] += 1
                before.append((signal, squares[signal]))
                nc.scalar.activation(ps[JUNK][:], src, ACT.Square, accum_out=dst).then_inc(signal, 1)

            def x_hi_part(step, g0):
                for s in range(KC // 2):
                    act.wait_ge(x_tr, 8 * step + s + 1)
                    for c in range(2):
                        k = 2 * s + c
                        ins = nc.scalar.activation(xT_hi[:, k, :], ps[TB[s % 3]][:, c * SEQ:(c + 1) * SEQ],
                                                   ACT.Copy, scale=vcol[:, g0 + k:g0 + k + 1])
                    ins.then_inc(x_hi, 1)
                    if step == 0 and 1 <= s <= AHEAD:
                        hi(s - 1)

            def x_square(k, step, n):
                for t in range(TOK):
                    if step:
                        act.wait_ge(xn_ok, TOK * DN * (step - 1) + TOK * n + t + 1)
                    square(ss[:, k, t, n:n + 1], x[:, t, n * NT:(n + 1) * NT], x_sq)

            def hidden_hi(f, j):
                for c in range(2):
                    act.wait_ge(h_tr, j * 2 + (2 * FTILES * f + 1 + c))
                    nc.scalar.activation(flat(hT_hi[:, bass.ds(j * 4 + 2 * c, 2), :]), ps[4 + c][:],
                                         ACT.Copy).then_inc(h_hi, 1)

            def up_tile(b, j):
                f, k, step = (0, 0, 0) if b == U1 else (1, 4, 2)
                first = isinstance(j, int)
                for h in range(16):
                    if first and 1 <= h <= DN:
                        x_square(k, step, h - 1)
                    if not first and h == 4:
                        hidden_hi(f, j - 1)
                    if h == 8:
                        act.wait_ge(w_used, j * 16 + (b + 8))
                        if first:
                            act.wait_ge(r_ok, k + 1)
                        for t in range(TOK):
                            nc.scalar.activation(nat[:, t, :], ps[t][:], ACT.Silu,
                                                 scale=rr[:, k, t:t + 1]).then_inc(silu_ok, 1)
                    hi(b + h + AHEAD, j)

            def up(b):
                up_tile(b, 0)
                with act.Fori(1, FTILES) as j:
                    up_tile(b, j)
                hidden_hi(0 if b == U1 else 1, FTILES - 1)

            def y_squares(k, done, i):
                act.wait_ge(w_used, done)
                for n in range(2):
                    for t in range(TOK):
                        square(ss[:, k, t, 2 * i + n:2 * i + n + 1], ps[2 * n + t][:], y_sq)

            def down(b, k):
                for i in range(2):
                    for h in range(FC):
                        hi(b + FC * i + h + AHEAD)
                    y_squares(k, b + FC * (i + 1), i)

            act.dma_start(vrow[G_FFN1:G_FFN1 + KC, :], g1pre_d.rearrange("a (c p) -> (a c) p", p=P)).then_inc(vec_in, 16)
            act.dma_start(vrow[G_MIX:G_MIX + KC, :], mixpre_d.rearrange("a (c p) -> (a c) p", p=P)).then_inc(vec_in, 16)
            act.dma_start(vrow[G_FFN2:G_FFN2 + KC, :], g2pre_d.rearrange("a (c p) -> (a c) p", p=P)).then_inc(vec_in, 16)
            act.dma_start(vrow[LB0:LB0 + 2 * HEADS, :], lb_d.rearrange("a (c p) -> (a c) p", p=P)).then_inc(vec_in, 16)
            act.dma_start(vrow[PSC:PSC + 8, :], psc_d.rearrange("a (c p) -> (a c) p", p=P)).then_inc(vec_in, 16)
            act.wait_ge(vcol_ok, 1)
            x_hi_part(0, G_FFN1)
            up(U1)
            down(D1, 1)
            x_hi_part(1, G_MIX)
            for p in range(8 * INTILES):
                t, h = p // 8, p % 8
                if 1 <= p <= DN:
                    x_square(2, 1, p - 1)
                if p == 6:
                    act.wait_ge(lb_in, 1)
                    nc.scalar.activation(lbt[:, 0:2, :], lbt[:, 0:2, :], ACT.Exp).then_inc(lb_exp, 1)
                if 1 <= t <= 4 and h == 4:
                    act.wait_ge(in_tr, t)
                    dst, fn = (T, ACT.Sigmoid) if t <= 2 else (qP, ACT.Copy)
                    h0 = 4 * ((t - 1) % 2)
                    for c in range(2):
                        nc.scalar.activation(flat(dst[:, h0 + 2 * c:h0 + 2 * c + 2, :]), ps[4 + c][:],
                                             fn).then_inc(in_ev, 1)
                if p == 65:
                    act.wait_ge(lev_done, len(LEVELS) + 2)
                    for c in range(2):
                        nc.scalar.activation(S[:, 4 * c:4 * c + 4, 2 * P:3 * P],
                                             ps[6 + c][:].rearrange("p (h t) -> p h t", h=4),
                                             ACT.Copy).then_inc(s_last, 1)
                if p == 68:
                    act.wait_ge(o_done, 1)
                    for c in range(4):
                        nc.scalar.activation(osq[:, c // 2, NT * (c % 2):NT * (c % 2 + 1)], ps[4 + c][:],
                                             ACT.Square).then_inc(o_sq, 1)
                if p == 73:
                    act.wait_ge(pool_mm, 1)
                    for c in range(2):
                        nc.scalar.activation(flat(pooledT[:, 2 * c:2 * c + 2, :]), ps[4 + c][:],
                                             ACT.Copy).then_inc(pool_ev, 1)
                if p == 76:
                    act.wait_ge(wp_mm, 1)
                    for c in range(8):
                        ins = nc.scalar.activation(yT_hi[:, 8 + c, :], ps[4 + c // 2][:, SEQ * (c % 2):SEQ * (c % 2 + 1)],
                                                   ACT.Copy, scale=vcol[:, PSC + c:PSC + c + 1])
                        if c % 2:
                            ins.then_inc(yp_hi, 1)
                hi(IN + p + AHEAD)
                if h == 7:
                    act.wait_ge(w_used, IN + 8 * t + 8)
                    if t == 0:
                        act.wait_ge(r_ok, 3)
                    if 1 <= t <= 3:
                        act.wait_ge(in_tr, t)
                    dst = nat if t < 4 else (v_sb, u_sb, sg)[(t - 4) // 2]
                    c0 = 0 if t < 4 else NT * (t % 2)
                    for b in range(TOK):
                        nc.scalar.activation(dst[:, b, c0:c0 + NT], ps[2 * (t % 2) + b][:],
                                             ACT.Silu if t >= 8 else ACT.Copy,
                                             scale=rr[:, 2, b:b + 1]).then_inc(nat_ok, 1)
            for i in range(2):
                for h in range(KC):
                    if i == 0 and h in (0, 4):
                        act.wait_ge(yr_tr, h // 4 + 1)
                        for c in range(2):
                            nc.scalar.activation(flat(yT_hi[:, h + 2 * c:h + 2 * c + 2, :]), ps[4 + h // 2 + c][:],
                                                 ACT.Copy).then_inc(yr_hi, 1)
                    hi(OUT + KC * i + h + AHEAD)
                y_squares(3, OUT + KC * (i + 1), i)
            x_hi_part(2, G_FFN2)
            up(U2)
            down(D2, 5)

        @block.vector
        def _(dve):
            count = [0]
            V = nc.vector

            def link(ins):
                count[0] += 1
                ins.then_inc(dv, 1)
                dve.wait_ge(dv, count[0])

            def lo(g, j=0):
                if isinstance(j, int) and g + 16 * j >= END:
                    return
                dve.wait_ge(hi_ready, j * 16 + (g + 1))
                V.tensor_tensor(wlo[:, g % RING, :], raw[:, g // 2 % RAW, 1024 * (g % 2):1024 * (g % 2 + 1)],
                                whi[:, g % RING, :].bitcast(f32), ALU.subtract).then_inc(lo_ready, 1)

            def x_lo_part(step, g0, s):
                dve.wait_ge(x_hi, 8 * step + s + 1)
                for c in range(2):
                    k = 2 * s + c
                    ins = V.scalar_tensor_tensor(out=xT_lo[:, k, :], in0=ps[TB[s % 3]][:, c * SEQ:(c + 1) * SEQ],
                                                 scalar=vcol[:, g0 + k:g0 + k + 1], in1=xT_hi[:, k, :].bitcast(f32),
                                                 op0=ALU.mult, op1=ALU.subtract)
                ins.then_inc(x_lo, 1)

            def mean_square(k, signal, n):
                dve.wait_ge(signal, n)
                link(V.tensor_reduce(out=ms[:, k, :], in_=ss[:, k, :, :], op=ALU.add, axis=AX.X))
                V.tensor_scalar(ms[:, k, :], ms[:, k, :], 1.0 / D, EPS, ALU.mult, ALU.add).then_inc(ms_ok, 1)

            def hidden_lo(f, j):
                for c in range(2):
                    dve.wait_ge(h_hi, j * 2 + (2 * FTILES * f + 1 + c))
                    V.tensor_tensor(flat(hT_lo[:, bass.ds(j * 4 + 2 * c, 2), :]), ps[4 + c][:],
                                    flat(hT_hi[:, bass.ds(j * 4 + 2 * c, 2), :]).bitcast(f32),
                                    ALU.subtract).then_inc(h_lo, 1)

            def up_tile(b, j):
                f, k, step = (0, 0, 0) if b == U1 else (1, 4, 2)
                first = isinstance(j, int)
                for h in range(16):
                    if first and h == 6:
                        mean_square(k, x_sq, TOK * DN * (step + 1))
                    if not first and h == 4:
                        hidden_lo(f, j - 1)
                    lo(b + h + AHEAD, j)
                dve.wait_ge(w_used, j * 16 + (b + 16))
                for t in range(TOK):
                    dve.wait_ge(silu_ok, j * 2 + (2 * FTILES * f + t + 1))
                    V.scalar_tensor_tensor(out=nat[:, t, :], in0=ps[2 + t][:], scalar=rr[:, k, t:t + 1],
                                           in1=nat[:, t, :], op0=ALU.mult, op1=ALU.mult).then_inc(h_ok, 1)

            def up(b):
                up_tile(b, 0)
                with dve.Fori(1, FTILES) as j:
                    up_tile(b, j)
                hidden_lo(0 if b == U1 else 1, FTILES - 1)

            def y_gain(d, i):
                for n in range(2):
                    for t in range(TOK):
                        dve.wait_ge(y_sq, 8 * d + 4 * i + 2 * n + t + 1)
                        c = 2 * i + n
                        V.tensor_tensor(yg[:, c, t, :], ps[2 * n + t][:], gpost[:, c * NT:(c + 1) * NT],
                                        ALU.mult).then_inc(y_free, 1)

            def residual(d, k, g0):
                mean_square(k, y_sq, 8 * (d + 1))
                dve.wait_ge(r_ok, k + 1)
                dve.wait_ge(y_free, 12 * (d + 1))

                for n in range(DN):
                    for t in range(TOK):
                        xt = x[:, t, n * NT:(n + 1) * NT]
                        V.scalar_tensor_tensor(out=xt, in0=yg[:, n, t, :], scalar=rr[:, k, t:t + 1], in1=xt,
                                               op0=ALU.mult, op1=ALU.add).then_inc(xn_ok, 1)
                    if g0 is not None and n:
                        x_lo_part(d + 1, g0, 2 * n - 2)
                        x_lo_part(d + 1, g0, 2 * n - 1)
                if g0 is not None:
                    x_lo_part(d + 1, g0, 2 * DN - 2)
                    x_lo_part(d + 1, g0, 2 * DN - 1)

            def down(b, d, k, g0):
                dve.wait_ge(gain_in, 16 * (d + 1))
                for i in range(2):
                    for h in range(FC):
                        lo(b + FC * i + h + AHEAD)
                    y_gain(d, i)
                residual(d, k, g0)

            dve.wait_ge(vcol_tr, 1)
            V.tensor_copy(vcol[:], ps[0][:, 0:VROWS]).then_inc(vcol_ok, 1)
            dve.wait_ge(vcol_ok, 1)
            for s in range(KC // 2):
                x_lo_part(0, G_FFN1, s)
                if 1 <= s <= AHEAD:
                    lo(s - 1)
            up(U1)
            down(D1, 0, 1, G_MIX)

            def level_pairs(tensor, m):
                return flat(tensor[:]).rearrange("p (g two m) -> p g two m", two=2, m=m)

            def take_level(li):
                m = LEVELS[li]
                dve.wait_ge(lev_done, li + 2)
                for c in range(2):
                    for q in range(4):
                        h = 4 * c + q
                        dst = S[:, h, 0:SEQ].rearrange("p (g two m) -> p g two m", two=2, m=m)[:, :, 1, :]
                        msk = mask[:, li, :].rearrange("p (g m) -> p g m", m=m).bitcast(i32)
                        V.copy_predicated(dst, msk, ps[6 + c][:, P * q:P * (q + 1)].rearrange("p (g m) -> p g m", m=m))

            def next_level(li):
                m = LEVELS[li]
                q, k, f = level_pairs(qP, m), level_pairs(kR, m), level_pairs(T, m)
                n = 1024 // m
                whole = [f[:, :, side, m - 1:m].broadcast_to([P, n, m]) for side in range(2)]
                V.tensor_tensor(q[:, :, 1, :], q[:, :, 1, :], whole[0], ALU.mult)
                ins = V.tensor_tensor(k[:, :, 0, :], k[:, :, 0, :], whole[1], ALU.mult)
                if li < len(LEVELS) - 1:
                    link(ins)
                    ins = V.tensor_tensor(f[:, :, 1, m - 1:m], f[:, :, 1, m - 1:m], f[:, :, 0, m - 1:m], ALU.mult)
                link(ins)

            for p in range(8 * INTILES):
                t, h = p // 8, p % 8
                if p == 4:
                    l0, l1, tmp, lb, omlb, rec = (lbt[:, n, :] for n in range(6))
                    link(V.tensor_tensor(tmp, vcol[:, LB0:LB0 + 8], vcol[:, LB1:LB1 + 8], ALU.max))
                    V.tensor_tensor(l0, vcol[:, LB0:LB0 + 8], tmp, ALU.subtract)
                    V.tensor_tensor(l1, vcol[:, LB1:LB1 + 8], tmp, ALU.subtract).then_inc(lb_in, 1)
                if p == 6:
                    mean_square(2, x_sq, TOK * DN * 2)
                if p == 9:
                    dve.wait_ge(lb_exp, 1)
                    link(V.tensor_tensor(tmp, l0, l1, ALU.add))
                    link(V.reciprocal(rec, tmp))
                    link(V.tensor_tensor(lb, l0, rec, ALU.mult))
                    link(V.tensor_scalar(omlb, lb, -1.0, 1.0, ALU.mult, ALU.add))
                if t in (1, 2) and h == 5:
                    dve.wait_ge(in_ev, 2 * t)
                    h0 = 4 * (t - 1)
                    for hh in range(h0, h0 + 4):
                        ins = V.tensor_scalar(T[:, hh, :], T[:, hh, :], omlb[:, hh:hh + 1], lb[:, hh:hh + 1],
                                              ALU.mult, ALU.add)
                    link(ins)
                    V.tensor_scalar(flat(kR[:, h0:h0 + 4, :]), flat(T[:, h0:h0 + 4, :]), -1.0, 1.0,
                                    ALU.mult, ALU.add).then_inc(fk_ok, 1)
                if p == 40:
                    dve.wait_ge(lev_done, 1)
                    for c in range(4):
                        for q in range(2):
                            V.tensor_tensor(S[:, 2 * c + q, 0:SEQ].rearrange("p (b t) -> p b t", b=2),
                                            ps[4 + c][:, SEQ * q:SEQ * (q + 1)].rearrange("p (b t) -> p b t", b=2),
                                            ident[:].unsqueeze(1).broadcast_to([P, 2, P]), ALU.mult)
                    link(V.tensor_tensor(flat(qP[:]), flat(qP[:]), flat(T[:]), ALU.mult))
                    V.sem_inc(lev_ready, 1)
                    dve.wait_ge(consts_ok, 1)
                if p > 40 and (p - 40) % 3 == 0 and (p - 40) // 3 <= len(LEVELS):
                    li = (p - 40) // 3 - 1
                    take_level(li)
                    next_level(li)
                    V.sem_inc(lev_ready, 1)
                if p == 69:
                    dve.wait_ge(o_sq, 4)
                    link(V.tensor_reduce(out=hss[:], in_=osq[:].rearrange("p t (h v) -> p t h v", v=P),
                                         op=ALU.add, axis=AX.X))
                    V.tensor_scalar(hms[:], hss[:], 1.0 / P, EPS, ALU.mult, ALU.add).then_inc(hms_ok, 1)
                if p == 70:
                    dve.wait_ge(hr_ok, 1)
                    for c in range(4):
                        b, h0 = c // 2, 4 * (c % 2)
                        V.tensor_tensor(orn[:, b, P * h0:P * (h0 + 4)].rearrange("p (h v) -> p h v", v=P),
                                        ps[4 + c][:].rearrange("p (h v) -> p h v", v=P),
                                        hrr[:, b, h0:h0 + 4].unsqueeze(2).broadcast_to([P, 4, P]),
                                        ALU.mult).then_inc(orn_ok, 1)
                if p == 71:
                    dve.wait_ge(mixw_in, 32)
                    dve.wait_ge(orn_ok, 4)
                    o3 = orn[:].rearrange("p t (h v) -> p (t h) v", v=P)
                    link(V.tensor_tensor(o3, o3, gn_sb[:].unsqueeze(1).broadcast_to([P, 2 * HEADS, P]), ALU.mult))
                if p == 73:
                    dve.wait_ge(pool_mm, 1)
                    for c in range(2, 4):
                        V.tensor_copy(flat(pooledT[:, 2 * c:2 * c + 2, :]), ps[4 + c][:]).then_inc(pool_ev, 1)
                if p == 75:
                    gate_heads = 0
                    dve.wait_ge(nat_ok, 18)
                    for b in range(TOK):
                        V.tensor_tensor(orn[:, b, 0:NT], orn[:, b, 0:NT], sg[:, b, 0:NT], ALU.mult).then_inc(yrec_ok, 1)
                if p == 77:
                    for c in range(4):
                        dve.wait_ge(yp_hi, c + 1)
                        for q in range(2):
                            n = 2 * c + q
                            ins = V.scalar_tensor_tensor(out=yT_lo[:, 8 + n, :], in0=ps[4 + c][:, SEQ * q:SEQ * (q + 1)],
                                                         scalar=vcol[:, PSC + n:PSC + n + 1],
                                                         in1=yT_hi[:, 8 + n, :].bitcast(f32),
                                                         op0=ALU.mult, op1=ALU.subtract)
                        ins.then_inc(yp_lo, 1)
                lo(IN + p + AHEAD)
            dve.wait_ge(nat_ok, 20)
            for b in range(TOK):
                V.tensor_tensor(orn[:, b, NT:DH], orn[:, b, NT:DH], sg[:, b, NT:DH], ALU.mult).then_inc(yrec_ok, 1)
            for i in range(2):
                for h in range(KC):
                    if i == 0 and h in (0, 4):
                        for c in range(2):
                            dve.wait_ge(yr_hi, h // 2 + c + 1)
                            V.tensor_tensor(flat(yT_lo[:, h + 2 * c:h + 2 * c + 2, :]), ps[4 + h // 2 + c][:],
                                            flat(yT_hi[:, h + 2 * c:h + 2 * c + 2, :]).bitcast(f32),
                                            ALU.subtract).then_inc(yr_lo, 1)
                    lo(OUT + KC * i + h + AHEAD)
                if i == 0:
                    dve.wait_ge(gain_in, 32)
                y_gain(1, i)
            residual(1, 3, G_FFN2)
            up(U2)
            down(D2, 2, 5, None)

        @block.tensor
        def _(pe):
            mm = nc.tensor.matmul

            def three(bank, a_hi, a_lo, s, c0, start, stop):
                mm(bank, a_hi, whi[:, s, c0:c0 + NT], start=start, stop=False)
                mm(bank, a_hi, wlo[:, s, c0:c0 + NT], start=False, stop=False)
                return mm(bank, a_lo, whi[:, s, c0:c0 + NT], start=False, stop=stop)

            def narrow_half(g, j, n, banks, wait=None):
                pe.wait_ge(lo_ready, j * 16 + (g + 1))
                for c in range(2):
                    k = 2 * n + c
                    for t in range(TOK):
                        ins = three(banks[t][:], xT_hi[:, k, t * P:(t + 1) * P], xT_lo[:, k, t * P:(t + 1) * P],
                                    g % RING, c * NT, k == 0, k == KC - 1)
                ins.then_inc(w_used, 1)

            def wide_half(g, pos, last, k, a_hi, a_lo, i=0, per=0, free=None):
                pe.wait_ge(lo_ready, i * per + (g + 1))
                for n in range(2):
                    for t in range(TOK):
                        if free is not None:
                            pe.wait_ge(y_free, i * 4 + (free + 2 * n + t + 1))
                        ins = three(ps[2 * n + t][:], a_hi[:, k, t * P:(t + 1) * P], a_lo[:, k, t * P:(t + 1) * P],
                                    g % RING, n * NT, pos == 0, pos == last)
                ins.then_inc(w_used, 1)

            def transpose_x(step):
                for s in range(KC // 2):
                    if step:
                        pe.wait_ge(xn_ok, 8 * (step - 1) + 2 * (s // 2) + 2)
                    elif s in (0, 4):
                        pe.wait_ge(x_in[s // 4], 16)
                    if 8 * step + s >= 3:
                        pe.wait_ge(x_lo, 8 * step + s - 2)
                    for c in range(2):
                        k = 2 * s + c
                        for t in range(TOK):
                            ins = nc.tensor.transpose(ps[TB[s % 3]][:, c * SEQ + t * P:c * SEQ + (t + 1) * P],
                                                      x[:, t, k * P:(k + 1) * P], ident[:])
                    ins.then_inc(x_tr, 1)

            def transpose_tile(src, c0, banks, signal, each):
                for c in range(2):
                    for q in range(2):
                        for t in range(TOK):
                            n = c0 + P * (2 * c + q)
                            ins = nc.tensor.transpose(ps[banks[c]][:, q * SEQ + t * P:q * SEQ + (t + 1) * P],
                                                      src[:, t, n:n + P], ident[:])
                    if each or c:
                        ins.then_inc(signal, 1)

            def hidden(f, j):
                pe.wait_ge(h_ok, j * 2 + (2 * FTILES * f + 2))
                if not isinstance(j, int) or j:
                    pe.wait_ge(h_lo, j * 2 + 2 * FTILES * f)
                transpose_tile(nat, 0, (4, 5), h_tr, True)

            def up_tile(b, j):
                f, step = (0, 0) if b == U1 else (1, 2)
                first = isinstance(j, int)
                for h in range(16):
                    if not first and h == 3:
                        hidden(f, j - 1)
                    if first and h < 8:
                        pe.wait_ge(x_lo, 8 * step + h + 1)
                    if h == 0 and (f or not first):
                        pe.wait_ge(silu_ok, j * 2 + 2 * FTILES * f)
                    if h == 8 and (f or not first):
                        pe.wait_ge(h_ok, j * 2 + 2 * FTILES * f)
                    narrow_half(b + h, j, h % 8, ps[0:2] if h < 8 else ps[2:4])

            def up(b):
                up_tile(b, 0)
                with pe.Fori(1, FTILES) as j:
                    up_tile(b, j)
                hidden(0 if b == U1 else 1, FTILES - 1)

            def down(b, d):
                pe.sem_inc(y_free, 4)
                f = 0 if b == D1 else 1
                pe.wait_ge(h_lo, 2 * FTILES * (f + 1) - 2)
                with pe.Fori(0, 2) as i:
                    for k in range(FC):
                        if k == FC - 4:
                            pe.wait_ge(h_lo, 2 * FTILES * (f + 1))
                        wide_half(b + k, k, FC - 1, k, hT_hi, hT_lo, i, FC, 12 * d if k == 0 else None)

            pe.wait_ge(ident_ok, 1)
            pe.wait_ge(vec_in, 80)
            nc.tensor.transpose(ps[0][:, 0:VROWS], vrow[0:VROWS, :], ident[0:VROWS, 0:VROWS]).then_inc(vcol_tr, 1)
            transpose_x(0)
            pe.wait_ge(vcol_ok, 1)
            up(U1)
            down(D1, 0)
            transpose_x(1)

            for p in range(8 * INTILES):
                t, h = p // 8, p % 8
                if t == 0:
                    pe.wait_ge(x_lo, 8 + h + 1)
                if h == 0 and t >= 2:
                    pe.wait_ge(nat_ok, 2 * (t - 1))
                narrow_half(IN + p, 0, h, ps[2 * (t % 2):2 * (t % 2) + 2])
                if 1 <= t <= 4 and h == 2:
                    pe.wait_ge(nat_ok, 2 * t)
                    if t > 1:
                        pe.wait_ge(in_ev, 2 * (t - 1))
                    transpose_tile(nat, 0, (4, 5), in_tr, False)
                if p == 37:
                    pe.wait_ge(in_ev, 8)
                    pe.wait_ge(fk_ok, 2)
                    for hh in range(HEADS):
                        for b in range(TOK):
                            n = 2 * hh + b
                            ins = mm(ps[4 + n // 4][:, P * (n % 4):P * (n % 4 + 1)], kR[:, hh, P * b:P * (b + 1)],
                                     qP[:, hh, P * b:P * (b + 1)], start=True, stop=True)
                    ins.then_inc(lev_done, 1)
                if p >= 41 and (p - 41) % 3 == 0 and (p - 41) // 3 < len(LEVELS):
                    li = (p - 41) // 3
                    m = LEVELS[li]
                    pe.wait_ge(lev_ready, li + 1)
                    for hh in range(HEADS):
                        for b in range(TOK):
                            n = 2 * hh + b
                            right = qP[:, hh, P * b:P * (b + 1)].rearrange("p (g two m) -> p g two m", two=2, m=m)
                            ins = mm(ps[6 + n // 8][:, 64 * (n % 8):64 * (n % 8 + 1)].rearrange("p (g m) -> p g m", m=m),
                                     kR[:, hh, P * b:P * (b + 1)], right[:, :, 1, :], start=True, stop=True)
                    ins.then_inc(lev_done, 1)
                if p == 62:
                    pe.wait_ge(lev_ready, len(LEVELS) + 1)
                    for hh in range(HEADS):
                        ins = mm(ps[6 + hh // 4][:, P * (hh % 4):P * (hh % 4 + 1)], kR[:, hh, 0:P],
                                 qP[:, hh, P:2 * P], start=True, stop=True)
                    ins.then_inc(lev_done, 1)
                if p == 66:
                    pe.wait_ge(s_last, 2)
                    pe.wait_ge(nat_ok, 12)
                    for hh in range(HEADS):
                        cols = slice(P * (hh % 4), P * (hh % 4 + 1))
                        vc = slice(P * hh, P * (hh + 1))
                        mm(ps[4 + hh // 4][:, cols], S[:, hh, 0:P], v_sb[:, 0, vc], start=True, stop=True)
                        mm(ps[6 + hh // 4][:, cols], S[:, hh, 2 * P:3 * P], v_sb[:, 0, vc], start=True, stop=False)
                        ins = mm(ps[6 + hh // 4][:, cols], S[:, hh, P:2 * P], v_sb[:, 1, vc], start=False, stop=True)
                    ins.then_inc(o_done, 1)
                if p == 71:
                    pe.wait_ge(orn_ok, 4)
                    pe.wait_ge(nat_ok, 16)
                    pe.wait_ge(consts_ok, 1)
                    for n in range(8):
                        dst = ps[4 + n // 2][:, SEQ * (n % 2):SEQ * (n % 2 + 1)]
                        mm(dst, u_sb[:, 0, P * n:P * (n + 1)], band[:, n // 2, 0:SEQ], start=True, stop=False)
                        ins = mm(dst[:, P:SEQ], u_sb[:, 1, P * n:P * (n + 1)], band[:, n // 2, SEQ:SEQ + P],
                                 start=False, stop=True)
                    ins.then_inc(pool_mm, 1)
                if p == 74:
                    pe.wait_ge(pool_ev, 4)
                    pe.wait_ge(mixw_in, 32)
                    for g in range(4):
                        for db in range(2):
                            for cb in range(2):
                                ins = mm(ps[4 + g][:, SEQ * db:SEQ * (db + 1)], wp_sb[:, 2 * g + cb, P * db:P * (db + 1)],
                                         pooledT[:, 2 * g + cb, :], start=cb == 0, stop=cb == 1)
                    ins.then_inc(wp_mm, 1)
                if p == 78:
                    pe.wait_ge(yrec_ok, 2)
                    pe.wait_ge(yp_lo, 4)
                    transpose_tile(orn, 0, (4, 5), yr_tr, False)
            pe.wait_ge(nat_ok, 20)
            for i in range(2):
                for h, k in enumerate(out_kc):
                    if i == 0 and h == 3:
                        pe.wait_ge(yrec_ok, 4)
                        transpose_tile(orn, NT, (6, 7), yr_tr, False)
                    if i == 0 and h in (8, 12):
                        pe.wait_ge(yr_lo, 2 * (h // 4 - 1))
                    if i == 0 and h == 0:
                        pe.sem_inc(y_free, 4)
                    wide_half(OUT + KC * i + h, h, KC - 1, k, yT_hi, yT_lo, 0, 0, 12 + 4 * i if h == 0 else None)
            transpose_x(2)
            up(U2)
            down(D2, 2)


_INS = ["x", "ffn1_pre_g", "ffn1_w_gate", "ffn1_w_up", "ffn1_w_down", "ffn1_post_g", "mix_pre_g", "w_in",
        "hgrn_lb_logits", "hgrn_g_norm", "w_pool", "pool_scale", "w_out", "mix_post_g", "ffn2_pre_g",
        "ffn2_w_gate", "ffn2_w_up", "ffn2_w_down", "ffn2_post_g"]
_OUTS = [((1, SEQ, D), "float32")]


def kernel(**inputs):
    import numpy as _np
    import concourse.bacc as _bacc
    from concourse import mybir as _mybir
    from concourse.bass_utils import run_bass_kernel_spmd as _run

    nc = _bacc.Bacc("TRN2", target_bir_lowering=False, num_devices=1)
    arrays, args = {}, []
    for name in _INS:
        a = _np.ascontiguousarray(inputs[name])
        arrays[f"in_{name}_dram"] = a
        args.append(nc.dram_tensor(f"in_{name}_dram", a.shape, _mybir.dt.from_np(a.dtype), kind="ExternalInput").ap())
    for i, (shape, dtype) in enumerate(_OUTS):
        dt = _mybir.dt.from_np(_np.dtype(dtype))
        args.append(nc.dram_tensor(f"out_{i}_dram", shape, dt, kind="ExternalOutput").ap())
    build(nc, *args)
    r = _run(nc, [arrays], core_ids=[0])
    return r.results[0]["out_0_dram"]
```

```python
import concourse.bass as bass
from concourse import mybir
from concourse.alu_op_type import AluOpType as ALU
from contextlib import ExitStack

P = 128
SEQ, D, FF = 256, 2048, 5632
TOK = SEQ // P
KC = D // P
FC = FF // P
NT = 512
FTILES = FF // NT
DN = D // NT
DH = D // 2
HEADS = DH // P
INTILES = 5 * DH // NT
WINDOWS = (2, 4, 8, 16)
WMAX = max(WINDOWS)
EPS = 1e-6
LEVELS = (1, 2, 4, 8, 16, 32, 64)

RAW = 4
RING = 4
AHEAD = RING - 1

U1 = 0
D1 = U1 + 16 * FTILES
IN = D1 + 2 * FC
OUT = IN + 8 * INTILES
U2 = OUT + 2 * KC
D2 = U2 + 16 * FTILES
END = D2 + 2 * FC

G_FFN1, G_MIX, G_FFN2, LB0, LB1, PSC = 0, 16, 32, 48, 56, 64
VROWS = 72
VEARLY = G_MIX

TB = (4, 5, 6)
JUNK = 7


def build(nc, x_d, g1pre_d, w1g_d, w1u_d, w1d_d, g1post_d, mixpre_d, win_d, lb_d, gnorm_d,
          wpool_d, psc_d, wout_d, mixpost_d, g2pre_d, w2g_d, w2u_d, w2d_d, g2post_d, out_d):
    f32 = mybir.dt.float32
    f32r = mybir.dt.float32r
    i32 = mybir.dt.int32
    ACT = mybir.ActivationFunctionType
    AX = mybir.AxisListType
    K = 1024
    base = (nc.sbuf_base + 63) // 64 * 64

    def at(name, kib, shape, dt=f32):
        return nc.alloc_sbuf_tensor_at(name, shape, dt, offset=base + int(kib * K))

    raw = at("raw", 0, [P, RAW, 2048])
    whi = at("whi", 32, [P, RING, 1024], f32r)
    wlo = at("wlo", 48, [P, RING, 1024], f32r)
    hT_hi = at("hT_hi", 64, [P, FC, SEQ], f32r)
    hT_lo = at("hT_lo", 108, [P, FC, SEQ], f32r)
    xT_hi = at("xT_hi", 152, [P, KC, SEQ], f32r)
    xT_lo = at("xT_lo", 168, [P, KC, SEQ], f32r)
    x = at("x", 184, [P, TOK, D])
    nat = at("nat", 200, [P, TOK, NT])
    ident = at("ident", 204, [P, P])
    vrow = at("vrow", 204.5, [P, P])
    vcol = at("vcol", 205, [P, VROWS])
    ss = at("ss", 205.5, [P, 6, TOK, DN])
    ms = at("ms", 205.75, [P, 6, TOK])
    rr = at("rr", 205.875, [P, 6, TOK])
    mhalf = at("mhalf", 206, [P, TOK * HEADS])
    lbt = at("lbt", 206.125, [P, 6, HEADS])
    hss = at("hss", 206.375, [P, TOK, HEADS])
    hms = at("hms", 206.5, [P, TOK, HEADS])
    hrr = at("hrr", 206.625, [P, TOK, HEADS])
    yg = at("yg", 152, [P, DN, TOK, NT])
    gpost = at("gpost", 168, [P, D])
    yT_hi = hT_hi
    yT_lo = hT_lo
    vrest = at("vrest", 64, [P, P])
    T = at("T", 64, [P, HEADS, SEQ])
    pooledT = at("pooledT", 64, [P, HEADS, SEQ])
    u_sb = at("u_sb", 72, [P, TOK, DH])
    qP = at("qP", 80, [P, HEADS, SEQ])
    osq = at("osq", 80, [P, TOK, DH])
    kR = at("kR", 88, [P, HEADS, SEQ])
    orn = at("orn", 88, [P, TOK, DH])
    v_sb = at("v_sb", 96, [P, TOK, DH])
    mask = at("mask", 104, [P, len(LEVELS), P])
    wp_sb = at("wp_sb", 108, [P, 8, 256])
    S = at("S", 124, [P, HEADS, 3 * P])
    sg = at("sg", 136, [P, TOK, DH])
    band = at("band", 144, [P, len(WINDOWS), SEQ + P])
    gn_sb = at("gn_sb", 150.5, [P, P])

    with ExitStack() as ctx:
        ps = [ctx.enter_context(nc.psum_tensor(f"ps{i}", [P, NT], f32)) for i in range(8)]

        def sem(name):
            return ctx.enter_context(nc.semaphore(name))

        raw_in = [sem(f"raw_in{i}") for i in range(RAW)]
        hi_ready, lo_ready = sem("hi_ready"), sem("lo_ready")
        w_used = sem("w_used")
        x_in = [sem(f"x_in{i}") for i in range(DN)]
        vec_in, vrest_in, gain_in, mixw_in = sem("vec_in"), sem("vrest_in"), sem("gain_in"), sem("mixw_in")
        ident_ok, consts_ok = sem("ident_ok"), sem("consts_ok")
        vcol_tr, vcol_ok = sem("vcol_tr"), sem("vcol_ok")
        silu_ok, h_ok = sem("silu_ok"), sem("h_ok")
        h_tr, h_hi, h_lo = sem("h_tr"), sem("h_hi"), sem("h_lo")
        y_done, y_free, y_sq = sem("y_done"), sem("y_free"), sem("y_sq")
        ms_ok, r_ok = sem("ms_ok"), sem("r_ok")
        xn_ok, x_sq = sem("xn_ok"), sem("x_sq")
        x_tr, x_hi, x_lo = sem("x_tr"), sem("x_hi"), sem("x_lo")
        dv, gp = sem("dv"), sem("gp")
        nat_ok, in_tr, in_ev, fk_ok = sem("nat_ok"), sem("in_tr"), sem("in_ev"), sem("fk_ok")
        lb_in, lb_exp = sem("lb_in"), sem("lb_exp")
        lev_ready, lev_done, s_last = sem("lev_ready"), sem("lev_done"), sem("s_last")
        o_done, o_sq, hms_ok, hr_ok, orn_ok = (sem(n) for n in ("o_done", "o_sq", "hms_ok", "hr_ok", "orn_ok"))
        pool_mm, pool_ev, wp_mm, yp_hi, yp_lo = (sem(n) for n in ("pool_mm", "pool_ev", "wp_mm", "yp_hi", "yp_lo"))
        yrec_ok, yr_tr, yr_hi, yr_lo = (sem(n) for n in ("yrec_ok", "yr_tr", "yr_hi", "yr_lo"))
        out_ok = sem("out_ok")

        block = ctx.enter_context(nc.Block())

        in_cols = [DH + NT * t for t in range(2)] + [NT * t for t in range(2)] + \
                  [2 * DH + NT * t for t in range(2)] + [4 * DH + NT * t for t in range(2)] + \
                  [3 * DH + NT * t for t in range(2)]
        out_kc = list(range(KC // 2, KC)) + list(range(KC // 2))

        def flat(ap):
            return ap.rearrange("p a b -> p (a b)")

        @block.sync
        def _(sp):
            def load(first_half, src, chunks, j=0):
                n = first_half // 2
                if not (isinstance(j, int) and first_half + 16 * j < 2 * RAW):
                    sp.wait_ge(lo_ready, j * 16 + (first_half - 2 * RAW + 2))
                dst = raw[:, n % RAW, :].rearrange("p (c f) -> p c f", c=chunks)
                sp.dma_start(dst, src).then_inc(raw_in[n % RAW], 16)

            def up_tile(b, j, wg, wu):
                for m, w in enumerate((wg, wu)):
                    rows = w[0].rearrange("(c p) f -> p c f", p=P)
                    for q in range(4):
                        if b == U1 and isinstance(j, int) and m == 0 and q:
                            load_x(q)
                        load(b + 8 * m + 2 * q, rows[:, 4 * q:4 * q + 4, bass.ds(j * NT, NT)], 4, j)

            def up(b, wg, wu):
                up_tile(b, 0, wg, wu)
                with sp.Fori(1, FTILES) as j:
                    up_tile(b, j, wg, wu)

            def down(b, w, order):
                rows = w[0].rearrange("(c p) n -> p c n", p=P)
                for i in range(2):
                    for n in range(0, len(order), 2):
                        load(b + len(order) * i + n, rows[:, order[n]:order[n] + 2, 1024 * i:1024 * (i + 1)], 2)

            xv = x_d[0].rearrange("(t p) d -> p t d", p=P)

            def load_x(n):
                cols = slice(n * NT, (n + 1) * NT)
                sp.dma_start(x[:, :, cols], xv[:, :, cols]).then_inc(x_in[n], 16)

            sp.dma_start(vrow[0:VEARLY, :], g1pre_d.rearrange("a (c p) -> (a c) p", p=P)).then_inc(vec_in, 16)
            load_x(0)
            up_tile(U1, 0, w1g_d, w1u_d)
            with sp.Fori(1, FTILES) as j:
                up_tile(U1, j, w1g_d, w1u_d)
            down(D1, w1d_d, list(range(FC)))
            rows = win_d[0].rearrange("(c p) f -> p c f", p=P)
            for t in range(INTILES):
                for q in range(4):
                    load(IN + 8 * t + 2 * q, rows[:, 4 * q:4 * q + 4, in_cols[t]:in_cols[t] + NT], 4)
            down(OUT, wout_d, out_kc)
            up(U2, w2g_d, w2u_d)
            down(D2, w2d_d, list(range(FC)))
            ov = out_d[0].rearrange("(t p) d -> p t d", p=P)
            for n in range(DN):
                sp.wait_ge(xn_ok, TOK * DN * 2 + TOK * (n + 1))
                sp.dma_start(ov[:, :, n * NT:(n + 1) * NT], x[:, :, n * NT:(n + 1) * NT]).then_inc(out_ok, 16)
            sp.wait_ge(out_ok, 16 * DN)

        @block.gpsimd
        def _(pool):
            count = [0]

            def link(ins):
                count[0] += 1
                ins.then_inc(gp, 1)
                pool.wait_ge(gp, count[0])

            link(nc.gpsimd.memset(ident[:], 0.0))
            nc.gpsimd.affine_select(out=ident[:], in_=ident[:], compare_op=ALU.not_equal, fill=1.0, base=0,
                                    pattern=[[-1, P]], channel_multiplier=1).then_inc(ident_ok, 1)
            link(nc.gpsimd.memset(mhalf[:], -0.5))

            def inv_root(k, half):
                pool.wait_ge(ms_ok, k + 1)
                ins = nc.gpsimd.tensor_tensor(rr[:, k, :], ms[:, k, :], mhalf[:, 0:TOK], ALU.pow)
                if half:
                    link(ins)
                    ins = nc.gpsimd.tensor_scalar(rr[:, k, :], rr[:, k, :], 0.5, None, ALU.mult)
                ins.then_inc(r_ok, 1)

            def load_gain(b, gain):
                pool.wait_ge(w_used, b)
                pool.dma_start(gpost[:], gain[0:1, :].broadcast_to([P, D])).then_inc(gain_in, 16)

            inv_root(0, False)
            load_gain(D1, g1post_d)
            inv_root(1, True)
            pool.wait_ge(w_used, IN)
            pool.dma_start(gn_sb[:], gnorm_d[0:1, :].broadcast_to([P, P])).then_inc(mixw_in, 16)
            pool.dma_start(wp_sb[:], wpool_d[0].rearrange("g (c p) d -> p (g c) d", p=P)).then_inc(mixw_in, 16)
            inv_root(2, False)
            for wi, w in enumerate(WINDOWS):
                link(nc.gpsimd.memset(band[:, wi, :], 1.0 / w))
                for t in range(w - 1):
                    link(nc.gpsimd.memset(band[:, wi, t:t + 1], 1.0 / (t + 1)))
                for c0, n in ((0, SEQ), (SEQ, P)):
                    b = band[:, wi, c0:c0 + n]
                    link(nc.gpsimd.affine_select(out=b, in_=b, compare_op=ALU.is_ge, fill=0.0, base=0,
                                                 pattern=[[1, n]], channel_multiplier=-1))
                    link(nc.gpsimd.affine_select(out=b, in_=b, compare_op=ALU.is_ge, fill=0.0, base=w - 1,
                                                 pattern=[[-1, n]], channel_multiplier=1))
                    link(nc.gpsimd.tensor_tensor(b[:, 0:P], b[:, 0:P], ident[:], ALU.subtract))
            for li, m in enumerate(LEVELS):
                link(nc.gpsimd.memset(mask[:, li, :], 1.0))
                n = P // (2 * m)
                for blk in range(2):
                    v = mask[:, li, 64 * blk:64 * blk + 64].rearrange("p (j m) -> p j m", m=m)
                    link(nc.gpsimd.affine_select(out=v, in_=v, compare_op=ALU.is_ge, fill=0.0, base=0,
                                                 pattern=[[-2 * m, n], [0, m]], channel_multiplier=1))
                    ins = nc.gpsimd.affine_select(out=v, in_=v, compare_op=ALU.is_ge, fill=0.0, base=m - 1,
                                                  pattern=[[2 * m, n], [0, m]], channel_multiplier=-1)
                    if li < len(LEVELS) - 1 or blk == 0:
                        link(ins)
            ins.then_inc(consts_ok, 1)
            pool.wait_ge(hms_ok, 1)
            nc.gpsimd.tensor_tensor(flat(hrr[:]), flat(hms[:]), mhalf[:], ALU.pow).then_inc(hr_ok, 1)
            load_gain(OUT, mixpost_d)
            inv_root(3, False)
            inv_root(4, False)
            load_gain(D2, g2post_d)
            inv_root(5, True)

        @block.scalar
        def _(act):
            def hi(g, j=0):
                if isinstance(j, int) and g + 16 * j >= END:
                    return
                act.wait_ge(raw_in[g // 2 % RAW], j * 32 + 16 * (g // 2 // RAW + 1))
                if not (isinstance(j, int) and g + 16 * j < RING):
                    act.wait_ge(w_used, j * 16 + (g - RING + 1))
                nc.scalar.activation(whi[:, g % RING, :], raw[:, g // 2 % RAW, 1024 * (g % 2):1024 * (g % 2 + 1)],
                                     ACT.Copy).then_inc(hi_ready, 1)

            squares = {x_sq: 0, y_sq: 0}
            before = []

            def square(dst, src, signal):
                if before:
                    act.wait_ge(*before[-1])
                squares[signal] += 1
                before.append((signal, squares[signal]))
                nc.scalar.activation(ps[JUNK][:], src, ACT.Square, accum_out=dst).then_inc(signal, 1)

            def x_hi_part(step, g0, s):
                act.wait_ge(x_tr, 8 * step + s + 1)
                for c in range(2):
                    k = 2 * s + c
                    ins = nc.scalar.activation(xT_hi[:, k, :], ps[TB[s % 3]][:, c * SEQ:(c + 1) * SEQ],
                                               ACT.Copy, scale=vcol[:, g0 + k:g0 + k + 1])
                ins.then_inc(x_hi, 1)

            def x_square(k, step, n):
                for t in range(TOK):
                    if step:
                        act.wait_ge(xn_ok, TOK * DN * (step - 1) + TOK * n + t + 1)
                    square(ss[:, k, t, n:n + 1], x[:, t, n * NT:(n + 1) * NT], x_sq)

            def hidden_hi(f, j):
                for c in range(2):
                    act.wait_ge(h_tr, j * 2 + (2 * FTILES * f + 1 + c))
                    nc.scalar.activation(flat(hT_hi[:, bass.ds(j * 4 + 2 * c, 2), :]), ps[4 + c][:],
                                         ACT.Copy).then_inc(h_hi, 1)

            def up_tile(b, j):
                f, k, step = (0, 0, 0) if b == U1 else (1, 4, 2)
                first = isinstance(j, int)
                for h in range(16):
                    if first and 6 <= h < 6 + DN:
                        x_square(k, step, h - 6)
                    if not first and h == 4:
                        hidden_hi(f, j - 1)
                    if h == (13 if first else 8):
                        act.wait_ge(w_used, j * 16 + (b + 8))
                        if first:
                            act.wait_ge(r_ok, k + 1)
                        for t in range(TOK):
                            nc.scalar.activation(nat[:, t, :], ps[t][:], ACT.Silu,
                                                 scale=rr[:, k, t:t + 1]).then_inc(silu_ok, 1)
                    hi(b + h + AHEAD, j)
                    if first and h < KC // 2 - 2:
                        x_hi_part(step, G_FFN2 if f else G_FFN1, h + 2)

            def up(b):
                up_tile(b, 0)
                with act.Fori(1, FTILES) as j:
                    up_tile(b, j)
                hidden_hi(0 if b == U1 else 1, FTILES - 1)

            def y_squares(k, d, b, i, n):
                if n:
                    act.wait_ge(w_used, b)
                else:
                    act.wait_ge(y_done, 2 * d + i + 1)
                for t in range(TOK):
                    square(ss[:, k, t, 2 * i + n:2 * i + n + 1], ps[2 * n + t][:], y_sq)

            def pair_end(k, d, b, i):
                y_squares(k, d, b, i, 0)
                y_squares(k, d, b, i, 1)
                hi(b + AHEAD - 1)

            def down(b, d, k):
                for i in range(2):
                    for h in range(FC - 1):
                        hi(b + FC * i + h + AHEAD)
                    pair_end(k, d, b + FC * (i + 1), i)

            for row, vec in ((G_MIX, mixpre_d), (G_FFN2, g2pre_d), (LB0, lb_d), (PSC, psc_d)):
                rows = vec.rearrange("a (c p) -> (a c) p", p=P)
                act.dma_start(vrest[row - VEARLY:row - VEARLY + rows.shape[0], :], rows).then_inc(vrest_in, 16)
            act.wait_ge(vcol_ok, 1)
            x_hi_part(0, G_FFN1, 0)
            x_hi_part(0, G_FFN1, 1)
            for g in range(AHEAD):
                hi(g)
            up(U1)
            down(D1, 0, 1)
            x_hi_part(1, G_MIX, 0)
            x_hi_part(1, G_MIX, 1)
            for p in range(8 * INTILES):
                t, h = p // 8, p % 8
                if 4 <= p < 4 + DN:
                    x_square(2, 1, p - 4)
                if p == 10:
                    act.wait_ge(lb_in, 1)
                    nc.scalar.activation(lbt[:, 0:2, :], lbt[:, 0:2, :], ACT.Exp).then_inc(lb_exp, 1)
                if 1 <= t <= 4 and h == 4:
                    act.wait_ge(in_tr, t)
                    dst, fn = (T, ACT.Sigmoid) if t <= 2 else (qP, ACT.Copy)
                    h0 = 4 * ((t - 1) % 2)
                    for c in range(2):
                        nc.scalar.activation(flat(dst[:, h0 + 2 * c:h0 + 2 * c + 2, :]), ps[4 + c][:],
                                             fn).then_inc(in_ev, 1)
                if p == 65:
                    act.wait_ge(lev_done, len(LEVELS) + 2)
                    for c in range(2):
                        nc.scalar.activation(S[:, 4 * c:4 * c + 4, 2 * P:3 * P],
                                             ps[6 + c][:].rearrange("p (h t) -> p h t", h=4),
                                             ACT.Copy).then_inc(s_last, 1)
                if p == 68:
                    act.wait_ge(o_done, 1)
                    for c in range(4):
                        nc.scalar.activation(osq[:, c // 2, NT * (c % 2):NT * (c % 2 + 1)], ps[4 + c][:],
                                             ACT.Square).then_inc(o_sq, 1)
                if p == 73:
                    act.wait_ge(pool_mm, 1)
                    for c in range(2):
                        nc.scalar.activation(flat(pooledT[:, 2 * c:2 * c + 2, :]), ps[4 + c][:],
                                             ACT.Copy).then_inc(pool_ev, 1)
                if p == 76:
                    act.wait_ge(wp_mm, 1)
                    for c in range(8):
                        ins = nc.scalar.activation(yT_hi[:, 8 + c, :], ps[4 + c // 2][:, SEQ * (c % 2):SEQ * (c % 2 + 1)],
                                                   ACT.Copy, scale=vcol[:, PSC + c:PSC + c + 1])
                        if c % 2:
                            ins.then_inc(yp_hi, 1)
                hi(IN + p + AHEAD)
                if p < KC // 2 - 2:
                    x_hi_part(1, G_MIX, p + 2)
                if h == 7:
                    act.wait_ge(w_used, IN + 8 * t + 8)
                    if t == 0:
                        act.wait_ge(r_ok, 3)
                    if 1 <= t <= 3:
                        act.wait_ge(in_tr, t)
                    dst = nat if t < 4 else (v_sb, u_sb, sg)[(t - 4) // 2]
                    c0 = 0 if t < 4 else NT * (t % 2)
                    for b in range(TOK):
                        nc.scalar.activation(dst[:, b, c0:c0 + NT], ps[2 * (t % 2) + b][:],
                                             ACT.Silu if t >= 8 else ACT.Copy,
                                             scale=rr[:, 2, b:b + 1]).then_inc(nat_ok, 1)
            for i in range(2):
                for h in range(KC):
                    if i == 0 and h in (0, 4):
                        act.wait_ge(yr_tr, h // 4 + 1)
                        for c in range(2):
                            nc.scalar.activation(flat(yT_hi[:, h + 2 * c:h + 2 * c + 2, :]), ps[4 + h // 2 + c][:],
                                                 ACT.Copy).then_inc(yr_hi, 1)
                    if h < KC - 1:
                        hi(OUT + KC * i + h + AHEAD)
                pair_end(3, 1, OUT + KC * (i + 1), i)
            x_hi_part(2, G_FFN2, 0)
            x_hi_part(2, G_FFN2, 1)
            up(U2)
            down(D2, 2, 5)

        @block.vector
        def _(dve):
            count = [0]
            V = nc.vector

            def link(ins):
                count[0] += 1
                ins.then_inc(dv, 1)
                dve.wait_ge(dv, count[0])

            def lo(g, j=0):
                if isinstance(j, int) and g + 16 * j >= END:
                    return
                dve.wait_ge(hi_ready, j * 16 + (g + 1))
                V.tensor_tensor(wlo[:, g % RING, :], raw[:, g // 2 % RAW, 1024 * (g % 2):1024 * (g % 2 + 1)],
                                whi[:, g % RING, :].bitcast(f32), ALU.subtract).then_inc(lo_ready, 1)

            def x_lo_part(step, g0, s):
                dve.wait_ge(x_hi, 8 * step + s + 1)
                for c in range(2):
                    k = 2 * s + c
                    ins = V.scalar_tensor_tensor(out=xT_lo[:, k, :], in0=ps[TB[s % 3]][:, c * SEQ:(c + 1) * SEQ],
                                                 scalar=vcol[:, g0 + k:g0 + k + 1], in1=xT_hi[:, k, :].bitcast(f32),
                                                 op0=ALU.mult, op1=ALU.subtract)
                ins.then_inc(x_lo, 1)

            def mean_square(k, signal, n):
                dve.wait_ge(signal, n)
                link(V.tensor_reduce(out=ms[:, k, :], in_=ss[:, k, :, :], op=ALU.add, axis=AX.X))
                V.tensor_scalar(ms[:, k, :], ms[:, k, :], 1.0 / D, EPS, ALU.mult, ALU.add).then_inc(ms_ok, 1)

            def hidden_lo(f, j):
                for c in range(2):
                    dve.wait_ge(h_hi, j * 2 + (2 * FTILES * f + 1 + c))
                    V.tensor_tensor(flat(hT_lo[:, bass.ds(j * 4 + 2 * c, 2), :]), ps[4 + c][:],
                                    flat(hT_hi[:, bass.ds(j * 4 + 2 * c, 2), :]).bitcast(f32),
                                    ALU.subtract).then_inc(h_lo, 1)

            def up_tile(b, j):
                f, k, step = (0, 0, 0) if b == U1 else (1, 4, 2)
                first = isinstance(j, int)
                for h in range(16):
                    if first and h == 11:
                        mean_square(k, x_sq, TOK * DN * (step + 1))
                    if not first and h == 4:
                        hidden_lo(f, j - 1)
                    lo(b + h + AHEAD, j)
                    if first:
                        x_after_half(step, 3, G_FFN2 if f else G_FFN1, h)
                dve.wait_ge(w_used, j * 16 + (b + 16))
                for t in range(TOK):
                    dve.wait_ge(silu_ok, j * 2 + (2 * FTILES * f + t + 1))
                    V.scalar_tensor_tensor(out=nat[:, t, :], in0=ps[2 + t][:], scalar=rr[:, k, t:t + 1],
                                           in1=nat[:, t, :], op0=ALU.mult, op1=ALU.mult).then_inc(h_ok, 1)

            def up(b):
                up_tile(b, 0)
                with dve.Fori(1, FTILES) as j:
                    up_tile(b, j)
                hidden_lo(0 if b == U1 else 1, FTILES - 1)

            def y_gain(d, i, tiles):
                for n, t in tiles:
                    dve.wait_ge(y_sq, 8 * d + 4 * i + 2 * n + t + 1)
                    c = 2 * i + n
                    V.tensor_tensor(yg[:, c, t, :], ps[2 * n + t][:], gpost[:, c * NT:(c + 1) * NT],
                                    ALU.mult).then_inc(y_free, 1)

            def pair_end(d, k, b, i, g0):
                y_gain(d, i, ((0, 0), (0, 1), (1, 0)))
                if i:
                    mean_square(k, y_sq, 8 * (d + 1))
                y_gain(d, i, ((1, 1),))
                if i:
                    residual(d, k, g0)
                lo(b + AHEAD - 1)

            def residual(d, k, g0):
                dve.wait_ge(r_ok, k + 1)
                dve.wait_ge(y_free, 12 * (d + 1))

                for n in range(2 if g0 is not None else DN):
                    residual_tile(k, n)
                if g0 is not None:
                    x_lo_part(d + 1, g0, 0)
                    x_lo_part(d + 1, g0, 1)

            def residual_tile(k, n):
                for t in range(TOK):
                    xt = x[:, t, n * NT:(n + 1) * NT]
                    V.scalar_tensor_tensor(out=xt, in0=yg[:, n, t, :], scalar=rr[:, k, t:t + 1], in1=xt,
                                           op0=ALU.mult, op1=ALU.add).then_inc(xn_ok, 1)

            def x_after_half(step, k, g0, h):
                if h < KC // 2 - 2:
                    x_lo_part(step, g0, h + 2)
                if step and h in (0, 2):
                    residual_tile(k, 2 + h // 2)

            def down(b, d, k, g0):
                dve.wait_ge(gain_in, 16 * (d + 1))
                for i in range(2):
                    for h in range(FC - 1):
                        lo(b + FC * i + h + AHEAD)
                    pair_end(d, k, b + FC * (i + 1), i, g0)

            dve.wait_ge(vcol_tr, 1)
            V.tensor_copy(vcol[:, 0:VEARLY], ps[0][:, 0:VEARLY]).then_inc(vcol_ok, 1)
            dve.wait_ge(vcol_ok, 1)
            x_lo_part(0, G_FFN1, 0)
            x_lo_part(0, G_FFN1, 1)
            for g in range(AHEAD):
                lo(g)
            dve.wait_ge(vcol_tr, 2)
            V.tensor_copy(vcol[:, VEARLY:VROWS], ps[3][:, 0:VROWS - VEARLY]).then_inc(vcol_ok, 1)
            up(U1)
            down(D1, 0, 1, G_MIX)

            def level_pairs(tensor, m):
                return flat(tensor[:]).rearrange("p (g two m) -> p g two m", two=2, m=m)

            def take_level(li):
                m = LEVELS[li]
                dve.wait_ge(lev_done, li + 2)
                for c in range(2):
                    for q in range(4):
                        h = 4 * c + q
                        dst = S[:, h, 0:SEQ].rearrange("p (g two m) -> p g two m", two=2, m=m)[:, :, 1, :]
                        msk = mask[:, li, :].rearrange("p (g m) -> p g m", m=m).bitcast(i32)
                        V.copy_predicated(dst, msk, ps[6 + c][:, P * q:P * (q + 1)].rearrange("p (g m) -> p g m", m=m))

            def next_level(li):
                m = LEVELS[li]
                q, k, f = level_pairs(qP, m), level_pairs(kR, m), level_pairs(T, m)
                n = 1024 // m
                whole = [f[:, :, side, m - 1:m].broadcast_to([P, n, m]) for side in range(2)]
                V.tensor_tensor(q[:, :, 1, :], q[:, :, 1, :], whole[0], ALU.mult)
                ins = V.tensor_tensor(k[:, :, 0, :], k[:, :, 0, :], whole[1], ALU.mult)
                if li < len(LEVELS) - 1:
                    link(ins)
                    ins = V.tensor_tensor(f[:, :, 1, m - 1:m], f[:, :, 1, m - 1:m], f[:, :, 0, m - 1:m], ALU.mult)
                link(ins)

            for p in range(8 * INTILES):
                t, h = p // 8, p % 8
                if p == 7:
                    l0, l1, tmp, lb, omlb, rec = (lbt[:, n, :] for n in range(6))
                    link(V.tensor_tensor(tmp, vcol[:, LB0:LB0 + 8], vcol[:, LB1:LB1 + 8], ALU.max))
                    V.tensor_tensor(l0, vcol[:, LB0:LB0 + 8], tmp, ALU.subtract)
                    V.tensor_tensor(l1, vcol[:, LB1:LB1 + 8], tmp, ALU.subtract).then_inc(lb_in, 1)
                if p == 8:
                    mean_square(2, x_sq, TOK * DN * 2)
                if p == 11:
                    dve.wait_ge(lb_exp, 1)
                    link(V.tensor_tensor(tmp, l0, l1, ALU.add))
                    link(V.reciprocal(rec, tmp))
                    link(V.tensor_tensor(lb, l0, rec, ALU.mult))
                    link(V.tensor_scalar(omlb, lb, -1.0, 1.0, ALU.mult, ALU.add))
                if t in (1, 2) and h == 5:
                    dve.wait_ge(in_ev, 2 * t)
                    h0 = 4 * (t - 1)
                    for hh in range(h0, h0 + 4):
                        ins = V.tensor_scalar(T[:, hh, :], T[:, hh, :], omlb[:, hh:hh + 1], lb[:, hh:hh + 1],
                                              ALU.mult, ALU.add)
                    link(ins)
                    V.tensor_scalar(flat(kR[:, h0:h0 + 4, :]), flat(T[:, h0:h0 + 4, :]), -1.0, 1.0,
                                    ALU.mult, ALU.add).then_inc(fk_ok, 1)
                if p == 40:
                    dve.wait_ge(lev_done, 1)
                    for c in range(4):
                        for q in range(2):
                            V.tensor_tensor(S[:, 2 * c + q, 0:SEQ].rearrange("p (b t) -> p b t", b=2),
                                            ps[4 + c][:, SEQ * q:SEQ * (q + 1)].rearrange("p (b t) -> p b t", b=2),
                                            ident[:].unsqueeze(1).broadcast_to([P, 2, P]), ALU.mult)
                    link(V.tensor_tensor(flat(qP[:]), flat(qP[:]), flat(T[:]), ALU.mult))
                    V.sem_inc(lev_ready, 1)
                    dve.wait_ge(consts_ok, 1)
                if p > 40 and (p - 40) % 3 == 0 and (p - 40) // 3 <= len(LEVELS):
                    li = (p - 40) // 3 - 1
                    take_level(li)
                    next_level(li)
                    V.sem_inc(lev_ready, 1)
                if p == 69:
                    dve.wait_ge(o_sq, 4)
                    link(V.tensor_reduce(out=hss[:], in_=osq[:].rearrange("p t (h v) -> p t h v", v=P),
                                         op=ALU.add, axis=AX.X))
                    V.tensor_scalar(hms[:], hss[:], 1.0 / P, EPS, ALU.mult, ALU.add).then_inc(hms_ok, 1)
                if p == 70:
                    dve.wait_ge(hr_ok, 1)
                    for c in range(4):
                        b, h0 = c // 2, 4 * (c % 2)
                        V.tensor_tensor(orn[:, b, P * h0:P * (h0 + 4)].rearrange("p (h v) -> p h v", v=P),
                                        ps[4 + c][:].rearrange("p (h v) -> p h v", v=P),
                                        hrr[:, b, h0:h0 + 4].unsqueeze(2).broadcast_to([P, 4, P]),
                                        ALU.mult).then_inc(orn_ok, 1)
                if p == 71:
                    dve.wait_ge(mixw_in, 32)
                    dve.wait_ge(orn_ok, 4)
                    o3 = orn[:].rearrange("p t (h v) -> p (t h) v", v=P)
                    link(V.tensor_tensor(o3, o3, gn_sb[:].unsqueeze(1).broadcast_to([P, 2 * HEADS, P]), ALU.mult))
                if p == 73:
                    dve.wait_ge(pool_mm, 1)
                    for c in range(2, 4):
                        V.tensor_copy(flat(pooledT[:, 2 * c:2 * c + 2, :]), ps[4 + c][:]).then_inc(pool_ev, 1)
                if p == 75:
                    dve.wait_ge(nat_ok, 18)
                    for b in range(TOK):
                        V.tensor_tensor(orn[:, b, 0:NT], orn[:, b, 0:NT], sg[:, b, 0:NT], ALU.mult).then_inc(yrec_ok, 1)
                if p == 77:
                    for c in range(4):
                        dve.wait_ge(yp_hi, c + 1)
                        for q in range(2):
                            n = 2 * c + q
                            ins = V.scalar_tensor_tensor(out=yT_lo[:, 8 + n, :], in0=ps[4 + c][:, SEQ * q:SEQ * (q + 1)],
                                                         scalar=vcol[:, PSC + n:PSC + n + 1],
                                                         in1=yT_hi[:, 8 + n, :].bitcast(f32),
                                                         op0=ALU.mult, op1=ALU.subtract)
                        ins.then_inc(yp_lo, 1)
                lo(IN + p + AHEAD)
                x_after_half(1, 1, G_MIX, p)
            dve.wait_ge(nat_ok, 20)
            for b in range(TOK):
                V.tensor_tensor(orn[:, b, NT:DH], orn[:, b, NT:DH], sg[:, b, NT:DH], ALU.mult).then_inc(yrec_ok, 1)
            for i in range(2):
                for h in range(KC):
                    if i == 0 and h in (0, 4):
                        for c in range(2):
                            dve.wait_ge(yr_hi, h // 2 + c + 1)
                            V.tensor_tensor(flat(yT_lo[:, h + 2 * c:h + 2 * c + 2, :]), ps[4 + h // 2 + c][:],
                                            flat(yT_hi[:, h + 2 * c:h + 2 * c + 2, :]).bitcast(f32),
                                            ALU.subtract).then_inc(yr_lo, 1)
                    if h < KC - 1:
                        lo(OUT + KC * i + h + AHEAD)
                if i == 0:
                    dve.wait_ge(gain_in, 32)
                pair_end(1, 3, OUT + KC * (i + 1), i, G_FFN2)
            up(U2)
            down(D2, 2, 5, None)

        @block.tensor
        def _(pe):
            mm = nc.tensor.matmul

            def three(bank, a_hi, a_lo, s, c0, start, stop):
                mm(bank, a_hi, whi[:, s, c0:c0 + NT], start=start, stop=False)
                mm(bank, a_hi, wlo[:, s, c0:c0 + NT], start=False, stop=False)
                return mm(bank, a_lo, whi[:, s, c0:c0 + NT], start=False, stop=stop)

            def narrow_half(g, j, n, banks, wait=None):
                pe.wait_ge(lo_ready, j * 16 + (g + 1))
                for c in range(2):
                    k = 2 * n + c
                    for t in range(TOK):
                        ins = three(banks[t][:], xT_hi[:, k, t * P:(t + 1) * P], xT_lo[:, k, t * P:(t + 1) * P],
                                    g % RING, c * NT, k == 0, k == KC - 1)
                ins.then_inc(w_used, 1)

            def wide_tile(g, n, first, last, k, a_hi, a_lo, i=0, free=None):
                for t in range(TOK):
                    if free is not None:
                        pe.wait_ge(y_free, i * 4 + (free + 2 * n + t + 1))
                    ins = three(ps[2 * n + t][:], a_hi[:, k, t * P:(t + 1) * P], a_lo[:, k, t * P:(t + 1) * P],
                                g % RING, n * NT, first, last)
                return ins

            def wide_pair(b, order, a_hi, a_lo, free, before, i=0, per=0):
                last = len(order) - 1
                for h, k in enumerate(order[:-2]):
                    before(h)
                    pe.wait_ge(lo_ready, i * per + (b + h + 1))
                    for n in range(2):
                        ins = wide_tile(b + h, n, h == 0, False, k, a_hi, a_lo, i, free if h == 0 else None)
                    ins.then_inc(w_used, 1)
                pe.wait_ge(lo_ready, i * per + (b + last + 1))
                for n in range(2):
                    for h in (last - 1, last):
                        ins = wide_tile(b + h, n, False, h == last, order[h], a_hi, a_lo)
                        if n and h < last:
                            ins.then_inc(w_used, 1)
                    if n == 0:
                        ins.then_inc(y_done, 1)
                ins.then_inc(w_used, 1)

            def transpose_x(step, s):
                if step:
                    pe.wait_ge(xn_ok, 8 * (step - 1) + 2 * (s // 2) + 2)
                elif s % 2 == 0:
                    pe.wait_ge(x_in[s // 2], 16)
                if 8 * step + s >= 3:
                    pe.wait_ge(x_lo, 8 * step + s - 2)
                for c in range(2):
                    k = 2 * s + c
                    for t in range(TOK):
                        ins = nc.tensor.transpose(ps[TB[s % 3]][:, c * SEQ + t * P:c * SEQ + (t + 1) * P],
                                                  x[:, t, k * P:(k + 1) * P], ident[:])
                ins.then_inc(x_tr, 1)

            def x_before_half(step, h):
                if h == 0:
                    transpose_x(step, 0)
                if h + 1 < KC // 2:
                    transpose_x(step, h + 1)
                pe.wait_ge(x_lo, 8 * step + h + 1)

            def transpose_tile(src, c0, banks, signal, each):
                for c in range(2):
                    for q in range(2):
                        for t in range(TOK):
                            n = c0 + P * (2 * c + q)
                            ins = nc.tensor.transpose(ps[banks[c]][:, q * SEQ + t * P:q * SEQ + (t + 1) * P],
                                                      src[:, t, n:n + P], ident[:])
                    if each or c:
                        ins.then_inc(signal, 1)

            def hidden(f, j):
                pe.wait_ge(h_ok, j * 2 + (2 * FTILES * f + 2))
                if not isinstance(j, int) or j:
                    pe.wait_ge(h_lo, j * 2 + 2 * FTILES * f)
                transpose_tile(nat, 0, (4, 5), h_tr, True)

            def up_tile(b, j):
                f, step = (0, 0) if b == U1 else (1, 2)
                first = isinstance(j, int)
                for h in range(16):
                    if not first and h == 3:
                        hidden(f, j - 1)
                    if first and h < 8:
                        x_before_half(step, h)
                    if first and not f and h == 1:
                        n = VROWS - VEARLY
                        pe.wait_ge(vrest_in, 64)
                        nc.tensor.transpose(ps[3][:, 0:n], vrest[0:n, :], ident[0:n, 0:n]).then_inc(vcol_tr, 1)
                    if first and not f and h == 8:
                        pe.wait_ge(vcol_ok, 2)
                    if h == 0 and (f or not first):
                        pe.wait_ge(silu_ok, j * 2 + 2 * FTILES * f)
                    if h == 8 and (f or not first):
                        pe.wait_ge(h_ok, j * 2 + 2 * FTILES * f)
                    narrow_half(b + h, j, h % 8, ps[0:2] if h < 8 else ps[2:4])

            def up(b):
                up_tile(b, 0)
                with pe.Fori(1, FTILES) as j:
                    up_tile(b, j)
                hidden(0 if b == U1 else 1, FTILES - 1)

            def down(b, d):
                pe.sem_inc(y_free, 4)
                f = 0 if b == D1 else 1
                pe.wait_ge(h_lo, 2 * FTILES * (f + 1) - 2)

                def before(h):
                    if h == FC - 4:
                        pe.wait_ge(h_lo, 2 * FTILES * (f + 1))

                with pe.Fori(0, 2) as i:
                    wide_pair(b, list(range(FC)), hT_hi, hT_lo, 12 * d, before, i, FC)

            pe.wait_ge(ident_ok, 1)
            pe.wait_ge(vec_in, 16)
            nc.tensor.transpose(ps[0][:, 0:VEARLY], vrow[0:VEARLY, :], ident[0:VEARLY, 0:VEARLY]).then_inc(vcol_tr, 1)
            up(U1)
            down(D1, 0)

            for p in range(8 * INTILES):
                t, h = p // 8, p % 8
                if t == 0:
                    x_before_half(1, h)
                if h == 0 and t >= 2:
                    pe.wait_ge(nat_ok, 2 * (t - 1))
                narrow_half(IN + p, 0, h, ps[2 * (t % 2):2 * (t % 2) + 2])
                if 1 <= t <= 4 and h == 2:
                    pe.wait_ge(nat_ok, 2 * t)
                    if t > 1:
                        pe.wait_ge(in_ev, 2 * (t - 1))
                    transpose_tile(nat, 0, (4, 5), in_tr, False)
                if p == 37:
                    pe.wait_ge(in_ev, 8)
                    pe.wait_ge(fk_ok, 2)
                    for hh in range(HEADS):
                        for b in range(TOK):
                            n = 2 * hh + b
                            ins = mm(ps[4 + n // 4][:, P * (n % 4):P * (n % 4 + 1)], kR[:, hh, P * b:P * (b + 1)],
                                     qP[:, hh, P * b:P * (b + 1)], start=True, stop=True)
                    ins.then_inc(lev_done, 1)
                if p >= 41 and (p - 41) % 3 == 0 and (p - 41) // 3 < len(LEVELS):
                    li = (p - 41) // 3
                    m = LEVELS[li]
                    pe.wait_ge(lev_ready, li + 1)
                    for hh in range(HEADS):
                        for b in range(TOK):
                            n = 2 * hh + b
                            right = qP[:, hh, P * b:P * (b + 1)].rearrange("p (g two m) -> p g two m", two=2, m=m)
                            ins = mm(ps[6 + n // 8][:, 64 * (n % 8):64 * (n % 8 + 1)].rearrange("p (g m) -> p g m", m=m),
                                     kR[:, hh, P * b:P * (b + 1)], right[:, :, 1, :], start=True, stop=True)
                    ins.then_inc(lev_done, 1)
                if p == 62:
                    pe.wait_ge(lev_ready, len(LEVELS) + 1)
                    for hh in range(HEADS):
                        ins = mm(ps[6 + hh // 4][:, P * (hh % 4):P * (hh % 4 + 1)], kR[:, hh, 0:P],
                                 qP[:, hh, P:2 * P], start=True, stop=True)
                    ins.then_inc(lev_done, 1)
                if p == 66:
                    pe.wait_ge(s_last, 2)
                    pe.wait_ge(nat_ok, 12)
                    for hh in range(HEADS):
                        cols = slice(P * (hh % 4), P * (hh % 4 + 1))
                        vc = slice(P * hh, P * (hh + 1))
                        mm(ps[4 + hh // 4][:, cols], S[:, hh, 0:P], v_sb[:, 0, vc], start=True, stop=True)
                        mm(ps[6 + hh // 4][:, cols], S[:, hh, 2 * P:3 * P], v_sb[:, 0, vc], start=True, stop=False)
                        ins = mm(ps[6 + hh // 4][:, cols], S[:, hh, P:2 * P], v_sb[:, 1, vc], start=False, stop=True)
                    ins.then_inc(o_done, 1)
                if p == 71:
                    pe.wait_ge(orn_ok, 4)
                    pe.wait_ge(nat_ok, 16)
                    pe.wait_ge(consts_ok, 1)
                    for n in range(8):
                        dst = ps[4 + n // 2][:, SEQ * (n % 2):SEQ * (n % 2 + 1)]
                        mm(dst, u_sb[:, 0, P * n:P * (n + 1)], band[:, n // 2, 0:SEQ], start=True, stop=False)
                        ins = mm(dst[:, P:SEQ], u_sb[:, 1, P * n:P * (n + 1)], band[:, n // 2, SEQ:SEQ + P],
                                 start=False, stop=True)
                    ins.then_inc(pool_mm, 1)
                if p == 74:
                    pe.wait_ge(pool_ev, 4)
                    pe.wait_ge(mixw_in, 32)
                    for g in range(4):
                        for db in range(2):
                            for cb in range(2):
                                ins = mm(ps[4 + g][:, SEQ * db:SEQ * (db + 1)], wp_sb[:, 2 * g + cb, P * db:P * (db + 1)],
                                         pooledT[:, 2 * g + cb, :], start=cb == 0, stop=cb == 1)
                    ins.then_inc(wp_mm, 1)
                if p == 78:
                    pe.wait_ge(yrec_ok, 2)
                    pe.wait_ge(yp_lo, 4)
                    transpose_tile(orn, 0, (4, 5), yr_tr, False)
            pe.wait_ge(nat_ok, 20)
            pe.sem_inc(y_free, 4)

            def before_first(h):
                if h == 3:
                    pe.wait_ge(yrec_ok, 4)
                    transpose_tile(orn, NT, (6, 7), yr_tr, False)
                if h in (8, 12):
                    pe.wait_ge(yr_lo, 2 * (h // 4 - 1))

            wide_pair(OUT, out_kc, yT_hi, yT_lo, 12, before_first)
            wide_pair(OUT + KC, out_kc, yT_hi, yT_lo, 16, lambda h: None)
            up(U2)
            down(D2, 2)


_INS = ["x", "ffn1_pre_g", "ffn1_w_gate", "ffn1_w_up", "ffn1_w_down", "ffn1_post_g", "mix_pre_g", "w_in",
        "hgrn_lb_logits", "hgrn_g_norm", "w_pool", "pool_scale", "w_out", "mix_post_g", "ffn2_pre_g",
        "ffn2_w_gate", "ffn2_w_up", "ffn2_w_down", "ffn2_post_g"]
_OUTS = [((1, SEQ, D), "float32")]


def kernel(**inputs):
    import numpy as _np
    import concourse.bacc as _bacc
    from concourse import mybir as _mybir
    from concourse.bass_utils import run_bass_kernel_spmd as _run

    nc = _bacc.Bacc("TRN2", target_bir_lowering=False, num_devices=1)
    arrays, args = {}, []
    for name in _INS:
        a = _np.ascontiguousarray(inputs[name])
        arrays[f"in_{name}_dram"] = a
        args.append(nc.dram_tensor(f"in_{name}_dram", a.shape, _mybir.dt.from_np(a.dtype), kind="ExternalInput").ap())
    for i, (shape, dtype) in enumerate(_OUTS):
        dt = _mybir.dt.from_np(_np.dtype(dtype))
        args.append(nc.dram_tensor(f"out_{i}_dram", shape, dt, kind="ExternalOutput").ap())
    build(nc, *args)
    r = _run(nc, [arrays], core_ids=[0])
    return r.results[0]["out_0_dram"]
```
